# Optimizing a Trainium2 kernel written in Bass

```python
import math
import jax, jax.numpy as jnp
from jax import lax
import numpy as np

D_MODEL = 1024
BATCH = 1
SEQ = 1024
DEPTH = 1

D_MIX = D_MODEL
SB_HEADS = 8
HEAD_DIM = 64
SB_WIDTH = SB_HEADS * HEAD_DIM
CONV_GROUPS = 8
CONV_WIDTH = D_MIX - SB_WIDTH
CONV_K = 3
SB_BLOCK = 128
N_KEYS = 128
N_EXPERTS = N_KEYS * N_KEYS
PEER_HEADS = 8
PEER_DK = 256
D_HALF = PEER_DK // 2
PEER_TOPK = 16
PEER_CHUNK = 128
EPS = 1e-6

kernel_name = "hymba_sb_conv_peer_block"

def rmsnorm(x, g):
    xf = x.astype(jnp.float32)
    y = xf * lax.rsqrt(jnp.mean(xf * xf, axis=-1, keepdims=True) + EPS)
    return (y * g.astype(jnp.float32)).astype(x.dtype)

def stick_breaking_attention(q, k, v):
    S = q.shape[2]
    scale = 1.0 / math.sqrt(q.shape[-1])
    outs = []
    for i in range(S // SB_BLOCK):
        t0 = i * SB_BLOCK
        L = t0 + SB_BLOCK
        qb = q[:, :, t0:L].astype(jnp.float32)
        kb = k[:, :, :L].astype(jnp.float32)
        vb = v[:, :, :L].astype(jnp.float32)
        z = jnp.einsum('bhqd,bhkd->bhqk', qb, kb) * scale
        t_pos = t0 + jnp.arange(SB_BLOCK)[:, None]
        s_pos = jnp.arange(L)[None, :]
        mask = s_pos < t_pos
        log_1m = jnp.where(mask, jax.nn.log_sigmoid(-z), 0.0)
        suffix = lax.cumsum(log_1m, axis=3, reverse=True) - log_1m
        a = jnp.where(mask, jnp.exp(jax.nn.log_sigmoid(z) + suffix), 0.0)
        outs.append(jnp.einsum('bhqk,bhkd->bhqd', a, vb))
    return jnp.concatenate(outs, axis=2).astype(q.dtype)

def short_gated_conv(gb, gc, hc, conv_w, conv_b):
    S = hc.shape[1]
    u = gc * hc
    up = jnp.pad(u, ((0, 0), (CONV_K - 1, 0), (0, 0)))
    y = sum(conv_w[j] * up[:, j:j + S] for j in range(CONV_K)) + conv_b
    return gb * y

def peer(xn, wq, keys, u_tab, v_tab):
    B, S, D = xn.shape
    xt = xn.reshape(-1, PEER_CHUNK, D)

    def chunk(xc):
        q = (xc @ wq).reshape(PEER_CHUNK, PEER_HEADS, PEER_DK).astype(jnp.float32)
        s1 = jnp.einsum('thd,hnd->thn', q[..., :D_HALF], keys[0].astype(jnp.float32))
        s2 = jnp.einsum('thd,hnd->thn', q[..., D_HALF:], keys[1].astype(jnp.float32))
        v1, i1 = lax.top_k(s1, PEER_TOPK)
        v2, i2 = lax.top_k(s2, PEER_TOPK)
        cand = (v1[..., :, None] + v2[..., None, :]).reshape(PEER_CHUNK, PEER_HEADS, PEER_TOPK * PEER_TOPK)
        cand_idx = (i1[..., :, None] * N_KEYS + i2[..., None, :]).reshape(PEER_CHUNK, PEER_HEADS, PEER_TOPK * PEER_TOPK)
        best, pos = lax.top_k(cand, PEER_TOPK)
        idx = jnp.take_along_axis(cand_idx, pos, axis=-1)
        g = jax.nn.softmax(best, axis=-1)
        u = u_tab[idx]
        act = jax.nn.gelu(jnp.einsum('td,thkd->thk', xc, u))
        w = g.astype(xc.dtype) * act
        return jnp.einsum('thk,thkd->td', w, v_tab[idx])

    return lax.map(chunk, xt).reshape(B, S, D)

def setup_inputs(seed: int = 0) -> dict:
    key = jax.random.key(seed)
    ks = jax.random.split(key, 14)
    f32 = jnp.float32
    nrm = lambda k, shape, s: jax.random.normal(k, shape, f32) * s
    gain = lambda k, shape: 1.0 + 0.02 * jax.random.normal(k, shape, f32)
    return {
        "x": jax.random.normal(ks[0], (BATCH, SEQ, D_MODEL), f32),
        "mix_norm_g": gain(ks[1], (DEPTH, D_MODEL)),
        "w_in": nrm(ks[2], (DEPTH, D_MODEL, 3 * SB_WIDTH + 3 * CONV_WIDTH), D_MODEL ** -0.5),
        "conv_w": nrm(ks[3], (DEPTH, CONV_K, CONV_WIDTH), 0.5),
        "conv_b": nrm(ks[4], (DEPTH, CONV_WIDTH), 0.02),
        "attn_out_g": gain(ks[5], (DEPTH, SB_WIDTH)),
        "conv_out_g": gain(ks[6], (DEPTH, CONV_WIDTH)),
        "w_out": nrm(ks[7], (DEPTH, D_MIX, D_MODEL), D_MIX ** -0.5),
        "ffn_norm_g": gain(ks[8], (DEPTH, D_MODEL)),
        "peer_wq": nrm(ks[9], (DEPTH, D_MODEL, PEER_HEADS * PEER_DK), D_MODEL ** -0.5),
        "peer_keys": nrm(ks[10], (DEPTH, 2, PEER_HEADS, N_KEYS, D_HALF), D_HALF ** -0.5),
        "peer_u": nrm(ks[11], (DEPTH, N_EXPERTS, D_MODEL), D_MODEL ** -0.5),
        "peer_v": nrm(ks[12], (DEPTH, N_EXPERTS, D_MODEL), 0.5),
        "final_norm_g": gain(ks[13], (D_MODEL,)),
    }

def reference(x, mix_norm_g, w_in, conv_w, conv_b, attn_out_g, conv_out_g, w_out,
              ffn_norm_g, peer_wq, peer_keys, peer_u, peer_v, final_norm_g):
    B, S, D = x.shape
    for layer in range(DEPTH):
        h = rmsnorm(x, mix_norm_g[layer])
        proj = h @ w_in[layer]
        q, k, v, gb, gc, hc = jnp.split(proj, 6, axis=-1)
        heads = lambda t: t.reshape(B, S, SB_HEADS, HEAD_DIM).transpose(0, 2, 1, 3)
        o_attn = stick_breaking_attention(heads(q), heads(k), heads(v))
        o_attn = o_attn.transpose(0, 2, 1, 3).reshape(B, S, SB_WIDTH)
        o_conv = short_gated_conv(gb, gc, hc, conv_w[layer], conv_b[layer])
        mixed = jnp.concatenate([rmsnorm(o_attn, attn_out_g[layer]),
                                 rmsnorm(o_conv, conv_out_g[layer])], axis=-1)
        x = x + mixed @ w_out[layer]
        xn = rmsnorm(x, ffn_norm_g[layer])
        x = x + peer(xn, peer_wq[layer], peer_keys[layer], peer_u[layer], peer_v[layer])
    return rmsnorm(x, final_norm_g)


_drawn_inputs = setup_inputs


def setup_inputs(seed=0):
    import zlib

    import numpy as np

    out = dict(_drawn_inputs(seed))
    spreads = {}
    factors = {}
    for name, (base, spread) in spreads.items():
        noise = np.random.default_rng([zlib.crc32(name.encode()), seed]).standard_normal(out[name].shape)
        drawn = base * np.exp(spread * noise) if base else spread * noise
        out[name] = __import__('jax').numpy.asarray(drawn.astype(out[name].dtype))
    for name, factor in factors.items():
        out[name] = (out[name] * factor).astype(out[name].dtype)
    return out
```

```python
from contextlib import ExitStack

import concourse.bass as bass
from concourse import mybir

F32 = mybir.dt.float32
BF16 = mybir.dt.bfloat16
U32 = mybir.dt.uint32
ALU = mybir.AluOpType
ACT = mybir.ActivationFunctionType
AX_X = mybir.AxisListType.X

P = 128
EPS = 1e-6
GELU_CUBE = 0.044715
GELU_SCALE = 1.5957691216057308
LOWEST = -3.0e38
MASKED = -1.0e30

D = 1024
KD = D // P
S = 1024
CHUNKS = S // P
BATCHES = [[0], [1, 2], [3, 4, 5], [6, 7]]
TMAX = max(len(b) for b in BATCHES) * P
HEADS, DH = 8, 64
W = HEADS * DH
JW = W // P
PH, TOPK, NKEYS = 8, 16, 128
LISTS = 2 * PH
SLOTS = PH * TOPK
GROUP = 4
GROUPS = SLOTS // GROUP
EARLY_PARTS = 1
PARTS = 3
RING = 2 * GROUP
PE_COLS = 512
BANKS = 6
WSLOTS = 8
KEYS_STAY = 2
KEEP = 4



def proj_tiles():
    return [(kind, j) for j in range(JW) for kind in ("k", "q", "v", "hc", "gc", "gb")]


def att_blocks(c):
    return [(c, half, b) for half in range(2) for b in range(c, -1, -1)]


def heads_per_search(bi):
    return 2 if bi == 0 else 4


def search(at, k, c, h):
    at(k, "dve", "pair_sums", c, h)
    at(k, "dve", "top_pairs", c, h, 0)
    if heads_per_search(batch_of(c)) == 4:
        at(k + 1, "dve", "top_pairs", c, h, 2)
    at(k + 2, "dve", "gate_start", c, h)
    at(k + 2, "act", "gate_exp", c, h)
    at(k + 2, "dve", "look_up", c, h)
    at(k + 3, "dve", "experts", c, h)


def front_steps(bi):
    chunks = BATCHES[bi]
    steps = {}

    def at(k, eng, *phase):
        steps.setdefault(k, []).append((eng, *phase))

    k = 0
    for c in chunks:
        at(k, "sp", "load_x", c)
        at(k, "act", "norm_x", c)
        at(k + 1, "pe", "turn_h", c)
        at(k + 2, "act", "store_h", c)
        k += 2
    k += 1
    for i, (kind, j) in enumerate(proj_tiles()):
        at(k, "pe", "proj", bi, i)
        if kind == "gc":
            at(k + 2, "dve", "gate_h", bi, j)
            at(k + 3, "act", "conv_tap2", bi, j)
        elif kind == "gb":
            at(k + 3, "dve", "conv_taps", bi, j)
        else:
            at(k + 2, "act", "store_proj", bi, i)
        k += 1
    k += 3
    if bi > 0:
        at(k, "sp", "load_x_again", chunks[0])
    done = k
    for c in chunks:
        for m in att_blocks(c):
            at(k, "pe", "att_z", m)
            at(k + 1, "act", "att_log", m)
            at(k + 2, "dve", "att_soft", m)
            at(k + 3, "pe", "att_suffix", m)
            if m[2] > 0:
                at(k + 4, "dve", "att_carry", m)
            at(k + 4, "act", "att_exp", m)
            at(k + 5, "pe", "att_out", m)
            k += 1
        d = max(k + 5, done)
        if c > chunks[0]:
            at(d, "sp", "load_x_again", c)
        at(d, "act", "square_mix", c)
        at(d + 1, "dve", "gain_mix", c)
        at(d + 1, "pe", "sum_mix", c)
        at(d + 1, "act", "root_mix", c)
        at(d + 2, "pe", "out_proj", c, 0)
        at(d + 3, "dve", "add_mix", c, 0)
        at(d + 3, "pe", "out_proj", c, 1)
        at(d + 4, "dve", "add_mix", c, 1)
        at(d + 5, "act", "square_x2", c)
        if bi > 0:
            d += 2
        at(d + 6, "dve", "norm_x2", c)
        at(d + 6, "sp", "spill", c)
        at(d + 7, "pe", "turn_xn", c)
        at(d + 8, "act", "store_xn", c)
        done = d + 9
        k = max(k, d - 5)
    k = max(k, done)
    if bi >= KEYS_STAY:
        at(k, "sp", "load_keys", bi)
    hs = heads_per_search(bi)
    for t in range(LISTS):
        at(k, "pe", "query", bi, t)
        at(k + 2, "act", "store_query", bi, t)
        at(k + 3, "pe", "key_scores", bi, t)
        at(k + 4, "dve", "top_keys", bi, t)
        k += 1
        if bi == 0 and (t + 1) % (2 * hs) == 0:
            search(at, k + 4, chunks[0], t // 2 + 1 - hs)
    if bi > 0:
        k += 4
        for c in chunks:
            for h in range(0, PH, hs):
                search(at, k, c, h)
                k += 4
    return [steps[i] for i in sorted(steps)]


COST = {"gate_h": 0.9, "conv_taps": 1.6, "att_soft": 0.8, "att_carry": 0.6, "gain_mix": 1.2, "add_mix": 1.3,
        "norm_x2": 1.2, "top_keys": 3.5, "pair_sums": 1.2, "top_pairs": 3.5, "gate_start": 0.8, "look_up": 5.5,
        "experts": 0.8, "proj": 2.6, "att_z": 0.5, "att_suffix": 1.0, "att_out": 0.5, "out_proj": 3.5,
        "query": 2.6, "key_scores": 0.4, "turn_h": 1.0, "turn_xn": 1.0, "att_log": 1.8, "att_exp": 0.5,
        "norm_x": 3.0, "store_h": 3.0, "square_x2": 4.0, "store_xn": 2.0, "square_mix": 3.5, "root_mix": 1.5}
LONG_STEP = 2.0
BY_TOKENS = ("proj", "query", "key_scores", "top_keys", "gate_h", "conv_taps")


def timeline():
    out = []
    def phases(step):
        return [("front", *ph) for ph in step]

    def weight(bi, step):
        time = {"dve": 0.0, "pe": 0.0, "act": 0.0, "sp": 0.0}
        for eng, name, *_ in step:
            scale = len(BATCHES[bi]) * P / TMAX if name in BY_TOKENS else 1.0
            time[eng] += COST.get(name, 0.3) * scale
        return 0.15 + max(time["dve"] / 2.3, time["pe"] / 2.9, time["act"] / 3.5)

    early, known, chunk0 = 0, 0, [(g, part) for g in range(GROUPS) for part in range(PARTS)]
    def dve_time(step):
        return sum(COST.get(name, 0.0) for eng, name, *_ in step if eng == "dve")

    for step in front_steps(0):
        out += phases(step)
        if known:
            for _ in range(EARLY_PARTS):
                if chunk0[early][0] < known:
                    out.append(("group", 0, *chunk0[early]))
                    early += 1
        for eng, name, *args in step:
            if name == "experts":
                if not known:
                    out.append(("front", "sp", "load_chunk", 0))
                known = (args[1] + heads_per_search(0)) * TOPK // GROUP
    steps = {bi: front_steps(bi) for bi in range(1, len(BATCHES))}
    total = {bi: sum(weight(bi, s) for s in st) for bi, st in steps.items()}
    span = {bi: (BATCHES[bi - 1][0], BATCHES[bi][0]) for bi in steps}
    spent = dict.fromkeys(steps, 0.0)
    nxt = dict.fromkeys(steps, 0)
    for c in range(CHUNKS):
        busy = next((bi for bi, (a, b) in span.items() if a <= c < b), None)
        if busy is None:
            out.append(("body", c, 0, 1))
            if c > 0:
                out += [("front", "sp", "load_final_gain", c - 1), ("front", "act", "final_root", c - 1),
                        ("front", "dve", "final_scale", c - 1), ("front", "sp", "store_y", c - 1)]
            if c + 1 < CHUNKS:
                out.append(("front", "sp", "load_chunk", c + 1))
            out.append(("body", c, 1, GROUPS // 2 - 2))
            out.append(("body", c, GROUPS // 2 - 1, 1))
        else:
            a, b = span[busy]
            for g in range(GROUPS):
                for part in range(PARTS):
                    done = ((c - a) * GROUPS + g) * PARTS + part + 1 - (early if c == 0 else 0)
                    if done <= 0:
                        continue
                    out.append(("group", c, g, part))
                    goal = total[busy] * (done + 0.01) / ((b - a) * GROUPS * PARTS - (early if c == 0 else 0))
                    while nxt[busy] < len(steps[busy]) and spent[busy] < goal:
                        if part == 1 and dve_time(steps[busy][nxt[busy]]) > LONG_STEP:
                            break
                        spent[busy] += weight(busy, steps[busy][nxt[busy]])
                        out += phases(steps[busy][nxt[busy]])
                        nxt[busy] += 1
                if g == (8 if c + 1 < b else GROUPS - 4):
                    out.append(("front", "sp", "load_chunk", c + 1))
                if g == 0 and c > 0:
                    out += [("front", "sp", "load_final_gain", c - 1), ("front", "act", "final_root", c - 1)]
                if g == 1 and c > 0:
                    out += [("front", "dve", "final_scale", c - 1), ("front", "sp", "store_y", c - 1)]
            if c + 1 == b:
                while nxt[busy] < len(steps[busy]):
                    out += phases(steps[busy][nxt[busy]])
                    nxt[busy] += 1
        out.append(("front", "dve", "final_sum", c))
    c = CHUNKS - 1
    out += [("front", "sp", "load_final_gain", c), ("front", "act", "final_root", c),
            ("front", "dve", "final_scale", c), ("front", "sp", "store_y", c)]
    return out


def wide_groups(line):
    start = {}
    for b in range(1, len(BATCHES)):
        c = BATCHES[b][0] - 1
        found = line.index(("front", "dve", "pair_sums", BATCHES[b][0], 0))
        start[c] = min(g for g in range(GROUPS) if ("group", c, g, 0) in line[found:])
    return start


def batch_of(c):
    return next(i for i, b in enumerate(BATCHES) if c in b)


def bank_uses(name, args):
    if name in ("turn_h", "turn_xn"):
        return [(name, args[0], i) for i in range(2)]
    if name == "turn_keys":
        return [(name, i) for i in range(4)]
    if name in ("proj", "query", "key_scores"):
        return [(name, *args)]
    if name == "att_z":
        return [("att", args[0])]
    if name == "sum_mix":
        return [("sum", args[0])]
    if name == "out_proj":
        return [("out", *args, part) for part in range(2)]
    return []


def bank_frees(name, args):
    if name == "store_h":
        return [("turn_h", args[0], i) for i in range(2)]
    if name == "store_xn":
        return [("turn_xn", args[0], i) for i in range(2)]
    if name == "store_keys":
        return [("turn_keys", i) for i in range(4)]
    if name == "store_proj":
        return [("proj", *args)]
    if name == "gate_h":
        return [("proj", args[0], proj_tiles().index(("gc", args[1])))]
    if name == "conv_taps":
        return [("proj", args[0], proj_tiles().index(("gb", args[1])))]
    if name == "att_exp":
        return [("att", args[0])]
    if name == "root_mix":
        return [("sum", args[0])]
    if name == "add_mix":
        return [("out", *args, part) for part in range(2)]
    if name == "store_query":
        return [("query", *args)]
    if name == "top_keys":
        return [("key_scores", *args)]
    return []


def build(nc, x, w_in, w_out, wq, keys, uv, cols_in, g_ffn, g_fin, out):
    line = timeline()
    wide_from = wide_groups(line)
    phases = [("pe", "turn_keys"), ("act", "store_keys")] + [ph[1:] for ph in line if ph[0] == "front"]

    use_no, bank_no, before, freed_by, free_count = {}, {}, {}, {}, {"act": 0, "dve": 0}
    turns, holder = {"all": 0, "att": 0, "mix": 0}, {}
    for eng, name, *args in phases:
        for u in bank_uses(name, args):
            use_no[u] = len(use_no)
            pool_of = "att" if u[0] == "att" else "mix" if u[0] in ("sum", "out", "turn_xn") else "all"
            choice = {"all": range(BANKS), "att": range(2, BANKS), "mix": range(2)}[pool_of]
            bank_no[u] = choice[turns[pool_of] % len(choice)]
            turns[pool_of] += 1
            before[u] = holder.get(bank_no[u])
            holder[bank_no[u]] = u
        for u in bank_frees(name, args):
            free_count[eng] += 1
            freed_by[u] = (eng, free_count[eng])

    per_batch = len(proj_tiles()) + KD + LISTS
    n_tiles = per_batch * len(BATCHES)
    loads = [(name, *args) for _, name, *args in phases if name in ("load_x", "load_x_again")]
    x_loads = {what: i + 1 for i, what in enumerate(loads)}
    searches = [(args[0], args[1]) for _, name, *args in phases if name == "experts"]
    search_no = {what: i + 1 for i, what in enumerate(searches)}

    def found(c, h):
        hs = heads_per_search(batch_of(c))
        return search_no[(c, h // hs * hs)]

    wt_proj = lambda bi, i: bi * per_batch + i
    wt_out = lambda bi, k: bi * per_batch + len(proj_tiles()) + k
    wt_query = lambda bi, t: bi * per_batch + len(proj_tiles()) + KD + t

    att_list = [m for b in BATCHES for c in b for m in att_blocks(c)]
    att_no = {m: i for i, m in enumerate(att_list)}
    carry_no = {m: i + 1 for i, m in enumerate(m for m in att_list if m[2] > 0)}

    with ExitStack() as ctx:
        def sb(name, shape, dt=F32):
            return ctx.enter_context(nc.sbuf_tensor(name, shape, dt))

        def sem(name):
            return ctx.enter_context(nc.semaphore(name))

        ring = sb("ring", [P, RING, 2 * D])
        wpool = sb("wpool", [P, WSLOTS, KD * P])
        kT = sb("kT", [P, JW, S])
        vN = sb("vN", [P, CHUNKS, W])
        hT = sb("hT", [P, KD, TMAX])
        qT = sb("qT", [P, JW, TMAX])
        ocT = sb("ocT", [P, JW, TMAX])
        xb = sb("xb", [P, 2, D])
        xn = sb("xn", [P, 2, D])
        acc = sb("acc", [P, 2, D])
        lt = sb("lt", [P, 2, 512])
        lb = sb("lb", [P, 2, 512])
        rs = sb("rs", [P, 512])
        ab = sb("ab", [P, 2, 512])
        srch = sb("srch", [P, 10 * 4 * TOPK])
        idx = sb("idx", [P, KEEP, SLOTS], U32)
        gate = sb("gate", [P, KEEP, SLOTS])
        cur_idx = sb("cur_idx", [P, RING], U32)
        diag = sb("diag", [P, 2, GROUP, P])
        ident = sb("ident", [P, P])
        neg_tri = sb("neg_tri", [P, P])
        neg_one = sb("neg_one", [P, 1])
        keep01 = sb("keep01", [P, P])
        bias_m = sb("bias_m", [P, P])
        ones = sb("ones", [P, 1])
        eps = sb("eps", [P, 1])
        iota16 = sb("iota16", [P, TOPK], BF16)
        ffn_gain = sb("ffn_gain", [P, D])
        cols = sb("cols", [P, 8 * JW])
        gm = cols[:, 0:KD]
        ga = cols[:, KD:KD + 2 * JW].rearrange("p (a j) -> p a j", a=2)
        cw = cols[:, 4 * JW:7 * JW].rearrange("p (a j) -> p a j", a=3)
        cb = cols[:, 7 * JW:8 * JW]
        tail = sb("tail", [P, JW, 2])
        st = sb("st", [P, 16])
        dots = sb("dots", [P, RING])
        g_sq = sb("g_sq", [P, RING])
        g_xg = sb("g_xg", [P, RING])
        g_cu = sb("g_cu", [P, RING])
        g_ex = sb("g_ex", [P, RING])
        g_de = sb("g_de", [P, RING])
        g_re = sb("g_re", [P, RING])
        g_w = sb("g_w", [P, RING])
        gs = sb("gs", [P, 3, PH])

        hflat = hT[:, :, :].rearrange("p k t -> p (k t)")
        oflat = ocT[:, :, :].rearrange("p k t -> p (k t)")
        xbflat = xb[:, :, :].rearrange("p a d -> p (a d)")
        key_src = ring[:, 0, :].rearrange("p (t n) -> p t n", t=LISTS)
        keys_home = vN[:, CHUNKS // 2:, :].rearrange("p c n -> p (c n)")
        key_dst = keys_home.rearrange("p (t n) -> p t n", t=LISTS)
        hcs = lb[:, 0, :]
        cu = rs[:, 0:TMAX + 2]
        ct = ab[:, 0, :]
        qt_tile = lambda t: qT[:, t % 2, :]

        def tk(c, half, what, h=None):
            lc = BATCHES[batch_of(c)].index(c)
            o = lc * 4 * SLOTS + (2 * half + what) * SLOTS
            v = oflat[:, o:o + SLOTS]
            if h is not None:
                v = v[:, h * TOPK:(h + 1) * TOPK]
            return v

        NPAIR = TOPK * TOPK
        left_pairs = lb[:, :, :].rearrange("p a t -> p (a t)")
        n4 = 4 * TOPK
        best, pos = srch[:, 0:n4], srch[:, n4:2 * n4].bitcast(U32)
        pos_ab = srch[:, 2 * n4:4 * n4].bitcast(U32)
        pos_f = srch[:, 4 * n4:5 * n4].bitcast(BF16)
        idx_f = srch[:, 5 * n4:6 * n4].bitcast(BF16)
        num = srch[:, 6 * n4:8 * n4]
        gdif, gexp = srch[:, 8 * n4:9 * n4], srch[:, 9 * n4:10 * n4]

        def big(c):
            if c == 0:
                return xn[:, 1, :], acc[:, 1, :]
            return hflat[:, 0:4 * NPAIR], hflat[:, 4 * NPAIR:8 * NPAIR]

        vacc = ctx.enter_context(nc.psum_tensor("vacc", [P, PE_COLS], F32))
        banks = [ctx.enter_context(nc.psum_tensor(f"bank{i}", [P, 512], F32)) for i in range(BANKS)]
        o_ps = ctx.enter_context(nc.psum_tensor("o_ps", [P, 512], F32))
        bank = lambda u: banks[bank_no[u]]

        x2_d = nc.dram_tensor("x2_scratch", (CHUNKS, P, D), F32).ap()
        xn_d = nc.dram_tensor("xn_scratch", (CHUNKS, P, D), F32).ap()
        keys_d = nc.dram_tensor("keys_scratch", (P, LISTS * NKEYS), F32).ap()

        s_const = sem("s_const")
        s_keyload = sem("s_keyload")
        s_keyspill = sem("s_keyspill")
        s_keysin = sem("s_keysin")
        s_pool0 = sem("s_pool0")
        s_pool = sem("s_pool")
        s_tail0 = sem("s_tail0")
        s_x = sem("s_x")
        s_ss = sem("s_ss")
        s_hn = sem("s_hn")
        s_w = [sem(f"s_w{i}") for i in range(WSLOTS)]
        s_full = sem("s_full")
        s_act_free = sem("s_act_free")
        s_dve_free = sem("s_dve_free")
        s_u = sem("s_u")
        s_tap2 = sem("s_tap2")
        s_cv = sem("s_cv")
        s_log = sem("s_log")
        s_lchain = sem("s_lchain")
        s_soft = sem("s_soft")
        s_schain = sem("s_schain")
        s_carry = sem("s_carry")
        s_sfx = sem("s_sfx")
        s_o = sem("s_o")
        s_sq = sem("s_sq")
        s_gain = sem("s_gain")
        s_r2 = sem("s_r2")
        s_fgain = sem("s_fgain")
        s_xn2 = sem("s_xn2")
        s_spx = sem("s_spx")
        s_tk = sem("s_tk")
        s_gd = sem("s_gd")
        s_ge = sem("s_ge")
        s_exp = sem("s_exp")
        s_chunk = [sem(f"s_chunk{i}") for i in range(2)]
        s_idx = sem("s_idx")
        s_go = sem("s_go")
        s_gat = [sem(f"s_gat{i}") for i in range(RING)]
        s_dot = sem("s_dot")
        s_gsq = sem("s_gsq")
        s_gxg = sem("s_gxg")
        s_gcu = sem("s_gcu")
        s_gex = sem("s_gex")
        s_gde = sem("s_gde")
        s_gre = sem("s_gre")
        s_gw = sem("s_gw")
        s_vd = sem("s_vd")
        s_diag = sem("s_diag")
        s_vp = sem("s_vp")
        s_fsum = sem("s_fsum")
        s_fsq = sem("s_fsq")
        s_fg = sem("s_fg")
        s_y = sem("s_y")
        s_out = sem("s_out")

        block = ctx.enter_context(nc.Block())

        N_SMALL = 8
        BODIES = GROUPS // 2

        def lc_of(c):
            return BATCHES[batch_of(c)].index(c)

        def span(c):
            return slice(lc_of(c) * P, (lc_of(c) + 1) * P)

        def is_wide(c, i, q):
            return c in wide_from and 2 * i + q >= wide_from[c]

        def gather_line(eng_group, eng_front, me):
            for kind, *rest in line:
                if kind == "front":
                    if rest[0] == me:
                        eng_front(rest[1], rest[2:])
                elif eng_group is None:
                    continue
                elif kind == "group":
                    c, g, part = rest
                    eng_group(c, g // 2, g % 2, part, g == 0, g == GROUPS - 1)
                else:
                    c, first, count = rest
                    if count == 1:
                        for q in range(2):
                            for part in range(PARTS):
                                eng_group(c, first, q, part, first == 0 and q == 0, first == BODIES - 1 and q == 1)
                    else:
                        yield c, first, count

        @block.sync
        def _(sp):
            sp.dma_start(cols[:, :], cols_in).then_inc(s_const, 16)
            for half in range(2):
                sp.dma_start(key_src.rearrange("p (h a) d -> p h a d", a=2)[:, :, half, :],
                             keys[0, half].rearrange("h n d -> n h d")).then_inc(s_keyload, 16)

            state = {"x": 0, "w": 0}

            def last_use(n):
                bi, i = divmod(n, per_batch)
                if i < len(proj_tiles()):
                    return ("proj", bi, i)
                if i < len(proj_tiles()) + KD:
                    return ("out", BATCHES[bi][-1], 1, 1)
                return ("query", bi, i - len(proj_tiles()) - KD)

            def load_w():
                n = state["w"]
                state["w"] += 1
                if n >= WSLOTS:
                    sp.wait_ge(s_full, use_no[last_use(n - WSLOTS)] + 1)
                i = n % per_batch
                if i < len(proj_tiles()):
                    kind, j = proj_tiles()[i]
                    col = {"q": 0, "k": 1, "v": 2, "gb": 3, "gc": 4, "hc": 5}[kind] * W + j * P
                    src = w_in[0, :, col:col + P].rearrange("(k p) n -> p k n", p=P)
                    dst = wpool[:, n % WSLOTS, :].rearrange("p (k n) -> p k n", k=KD)
                elif i < len(proj_tiles()) + KD:
                    k = i - len(proj_tiles())
                    src = w_out[0, k * P:(k + 1) * P, :]
                    dst = wpool[:, n % WSLOTS, :]
                else:
                    t = i - len(proj_tiles()) - KD
                    src = wq[0, :, t * P:(t + 1) * P].rearrange("(k p) n -> p k n", p=P)
                    dst = wpool[:, n % WSLOTS, :].rearrange("p (k n) -> p k n", k=KD)
                sp.dma_start(dst, src).then_inc(s_w[n % WSLOTS], 16)

            def front(name, args):
                if name == "load_x":
                    c, = args
                    first_of_batch = c == BATCHES[batch_of(c)][0]
                    if c > 0:
                        sp.wait_ge(s_hn, c)
                    if first_of_batch and c > 0:
                        sp.wait_ge(s_full, use_no[("key_scores", batch_of(c) - 1, LISTS - 1)] + 1)
                    sp.dma_start(xb[:, 0, :], x[0, c * P:(c + 1) * P, :]).then_inc(s_x, 16)
                elif name == "load_x_again":
                    c, = args
                    if c > BATCHES[batch_of(c)][0]:
                        sp.wait_ge(s_spx, 32 * c)
                    else:
                        sp.wait_ge(s_hn, BATCHES[batch_of(c)][-1] + 1)
                    sp.dma_start(xb[:, 0, :], x[0, c * P:(c + 1) * P, :]).then_inc(s_x, 16)
                elif name == "spill":
                    c, = args
                    sp.wait_ge(s_xn2, c + 1)
                    sp.dma_start(x2_d[c], xb[:, 0, :]).then_inc(s_spx, 16)
                    sp.dma_start(xn_d[c], xb[:, 1, :]).then_inc(s_spx, 16)
                elif name == "load_keys":
                    bi, = args
                    c = BATCHES[bi][-1]
                    sp.wait_ge(s_keyspill, 16)
                    sp.wait_ge(s_spx, 32 * (c + 1))
                    sp.wait_ge(s_full, use_no[("turn_xn", c, 1)] + 1)
                    sp.dma_start(xbflat, keys_d).then_inc(s_keysin, 16)
                elif name == "load_chunk":
                    c, = args
                    if c >= 2:
                        sp.wait_ge(s_y, c - 1)
                        sp.wait_ge(s_out, 16 * (c - 1))
                    if c == 1:
                        sp.wait_ge(s_exp, found(0, PH - 1))
                    sp.wait_ge(s_spx, 32 * (c + 1))
                    sp.dma_start(xn[:, c % 2, :], xn_d[c]).then_inc(s_chunk[c % 2], 16)
                    sp.dma_start(acc[:, c % 2, :], x2_d[c]).then_inc(s_chunk[c % 2], 16)
                elif name == "load_final_gain":
                    c, = args
                    sp.wait_ge(s_fsq, c + 1)
                    sp.dma_start(xn[:, c % 2, :], bcast_rows(g_fin)).then_inc(s_fg, 16)
                elif name == "store_y":
                    c, = args
                    sp.wait_ge(s_y, c + 1)
                    sp.dma_start(out[0, c * P:(c + 1) * P, :], acc[:, c % 2, :]).then_inc(s_out, 16)

            def bcast_rows(g):
                return g.rearrange("o d -> (o d)").partition_broadcast(P)

            used = 0
            spill_keys = False
            for kind, *rest in line:
                if kind != "front":
                    continue
                eng, name, *args = rest
                if eng == "sp":
                    if name == "load_x" and args[0] == 0:
                        front(name, args)
                        while state["w"] < WSLOTS:
                            load_w()
                        sp.dma_start(ffn_gain[:, :], bcast_rows(g_ffn)).then_inc(s_fgain, 16)
                    else:
                        front(name, args)
                    if not spill_keys and name == "spill":
                        sp.wait_ge(s_act_free, 4)
                        sp.dma_start(keys_d, keys_home).then_inc(s_keyspill, 16)
                        spill_keys = True
                if eng == "pe":
                    if name in ("proj", "query"):
                        used += 1
                    if name == "out_proj" and args[1] == 1 and args[0] == BATCHES[batch_of(args[0])][-1]:
                        used += KD
                    while state["w"] < min(n_tiles, used + WSLOTS):
                        load_w()
            sp.wait_ge(s_out, 16 * CHUNKS)

        @block.gpsimd
        def _(pool):
            zeroed = [(ident, 0.0), (neg_tri, -1.0), (keep01, 1.0), (bias_m, 0.0)]
            for t, v in zeroed:
                nc.gpsimd.memset(t[:, :], v).then_inc(s_pool0, 1)
            nc.gpsimd.memset(neg_one[:, :], -1.0).then_inc(s_pool, 1)
            nc.gpsimd.memset(ones[:, :], 1.0).then_inc(s_pool, 1)
            nc.gpsimd.memset(eps[:, :], EPS).then_inc(s_pool, 1)
            nc.gpsimd.iota(iota16[:, :], pattern=[[1, TOPK]], base=0, channel_multiplier=0,
                           allow_small_or_imprecise_dtypes=True).then_inc(s_pool, 1)
            pool.wait_ge(s_pool0, len(zeroed))
            nc.gpsimd.affine_select(out=ident[:, :], in_=ident[:, :], compare_op=ALU.not_equal, fill=1.0, base=0,
                                    pattern=[[-1, P]], channel_multiplier=1).then_inc(s_pool, 1)
            nc.gpsimd.affine_select(out=neg_tri[:, :], in_=neg_tri[:, :], compare_op=ALU.is_ge, fill=0.0, base=0,
                                    pattern=[[-1, P]], channel_multiplier=1).then_inc(s_pool, 1)
            nc.gpsimd.affine_select(out=keep01[:, :], in_=keep01[:, :], compare_op=ALU.is_gt, fill=0.0, base=0,
                                    pattern=[[1, P]], channel_multiplier=-1).then_inc(s_pool, 1)
            nc.gpsimd.affine_select(out=bias_m[:, :], in_=bias_m[:, :], compare_op=ALU.is_gt, fill=MASKED, base=0,
                                    pattern=[[1, P]], channel_multiplier=-1).then_inc(s_pool, 1)

            def group(c, i, q, part, first, last):
                if part:
                    return
                n = i + c * BODIES
                h = (2 * i + q) * GROUP // TOPK if isinstance(i, int) else PH - 1
                pool.wait_ge(s_exp, found(c, h))
                used = (n * 2 + q - 2) * GROUP
                very_first = c == 0 and isinstance(i, int) and i == 0
                if not very_first:
                    pool.wait_ge(s_vd, used + 1)
                sl = slice(q * GROUP, (q + 1) * GROUP)
                nc.gpsimd.tensor_copy(cur_idx[:, sl], idx[:, c % KEEP, bass.ds(i * RING + q * GROUP, GROUP)])\
                    .then_inc(s_idx, 1)
                pool.wait_ge(s_idx, n * 2 + q + 1)
                pool.sem_inc(s_go, 1)
                for s in range(q * GROUP, (q + 1) * GROUP):
                    if not very_first:
                        pool.wait_ge(s_vd, used + s % GROUP + 1)
                        pool.wait_ge(s_vp, used + s % GROUP + 1)
                        pool.sem_inc(s_go, 1)
                    nc.gpsimd.indirect_dma_start(ring[:, s, :], None, uv,
                                                 bass.IndirectOffsetOnAxis(ap=cur_idx[:, s:s + 1], axis=0))\
                        .then_inc(s_gat[s], 16)

            for c, first, count in gather_line(group, None, "pool"):
                with pool.Fori(first, first + count) as i:
                    for q in range(2):
                        for part in range(PARTS):
                            group(c, i, q, part, False, False)

        @block.scalar
        def _(act):
            chain = {"ss": 0, "l": 0}

            def ss(ins):
                chain["ss"] += 1
                ins.then_inc(s_ss, 1)
                act.wait_ge(s_ss, chain["ss"])

            def inv_root(dst, src, n, done):
                ss(nc.scalar.activation(dst, src, ACT.Ln, bias=eps[:, 0:1], scale=1.0 / n))
                nc.scalar.activation(dst, dst, ACT.Exp, scale=-0.5).then_inc(done, 1)

            def group(c, i, q, part, first, last):
                if part == 0:
                    return
                n = i + c * BODIES
                sl = slice(q * GROUP, (q + 1) * GROUP)
                if part == 1:
                    act.wait_ge(s_gcu, n * 2 + q + 1)
                    nc.scalar.activation(g_ex[:, sl], g_cu[:, sl], ACT.Exp, scale=-GELU_SCALE * GELU_CUBE)\
                        .then_inc(s_gex, 1)
                    return
                act.wait_ge(s_gw, n * 2 + q + 1)
                for s in range(GROUP):
                    ins = nc.scalar.activation(diag[:, q, s, :], ident[:, :], ACT.Copy,
                                               scale=g_w[:, q * GROUP + s:q * GROUP + s + 1])
                ins.then_inc(s_diag, 1)

            def front(name, args):
                if name == "norm_x":
                    c, = args
                    bi = batch_of(c)
                    if c == 0:
                        act.wait_ge(s_pool, 8)
                        act.wait_ge(s_const, 16)
                    act.wait_ge(s_x, 16 * x_loads[("load_x", c)])
                    if c - 1 in BATCHES[bi]:
                        act.wait_ge(s_full, use_no[("turn_h", c - 1, 1)] + 1)
                    ss(nc.scalar.activation(xb[:, 1, :], xb[:, 0, :], ACT.Square, accum_out=st[:, 0:1]))
                    ss(nc.scalar.activation(st[:, 1:2], st[:, 0:1], ACT.Ln, bias=eps[:, 0:1], scale=1.0 / D))
                    ss(nc.scalar.activation(st[:, 2:3], st[:, 1:2], ACT.Exp, scale=-0.5))
                    nc.scalar.activation(xb[:, 1, :], xb[:, 0, :], ACT.Copy, scale=st[:, 2:3]).then_inc(s_hn, 1)
                elif name == "store_h":
                    c, = args
                    if c > 0:
                        act.wait_ge(s_exp, found(BATCHES[batch_of(c)][0] - 1, PH - 1))
                    for k in range(KD):
                        u = ("turn_h", c, k // 4)
                        if k % 4 == 0:
                            act.wait_ge(s_full, use_no[u] + 1)
                        ins = nc.scalar.activation(hT[:, k, span(c)], bank(u)[:, (k % 4) * P:(k % 4 + 1) * P],
                                                   ACT.Copy, scale=gm[:, k:k + 1])
                        if k % 4 == 3:
                            ins.then_inc(s_act_free, 1)
                elif name == "store_proj":
                    bi, t = args
                    kind, j = proj_tiles()[t]
                    chunks = BATCHES[bi]
                    T = len(chunks) * P
                    u = ("proj", bi, t)
                    act.wait_ge(s_full, use_no[u] + 1)
                    src = bank(u)[:, 0:T]
                    if kind == "k":
                        ins = nc.scalar.activation(kT[:, j, chunks[0] * P:chunks[0] * P + T], src, ACT.Copy)
                    elif kind == "q":
                        ins = nc.scalar.activation(qT[:, j, 0:T], src, ACT.Copy, scale=DH ** -0.5)
                    elif kind == "v":
                        if bi == KEYS_STAY:
                            act.wait_ge(s_keyspill, 16)
                        ins = nc.scalar.activation(vN[:, chunks[0]:chunks[0] + len(chunks), j * P:(j + 1) * P],
                                                   src.rearrange("p (c n) -> p c n", n=P), ACT.Copy)
                    else:
                        if bi + j > 0:
                            act.wait_ge(s_u, bi * JW + j)
                        ins = nc.scalar.activation(hcs[:, 0:T], src, ACT.Copy)
                    ins.then_inc(s_act_free, 1)
                elif name == "conv_tap2":
                    bi, j = args
                    T = len(BATCHES[bi]) * P
                    act.wait_ge(s_u, bi * JW + j + 1)
                    nc.scalar.activation(ct[:, 0:T], cu[:, 2:2 + T], ACT.Identity, bias=cb[:, j:j + 1],
                                         scale=cw[:, 2, j:j + 1]).then_inc(s_tap2, 1)
                elif name == "att_log":
                    m, = args
                    i = att_no[m]
                    act.wait_ge(s_full, use_no[("att", m)] + 1)
                    if i > 1:
                        act.wait_ge(s_soft, i - 1)
                    lg = lt[:, i % 2, :]
                    z = bank(("att", m))[:, :]
                    chain["l"] += 1
                    nc.scalar.activation(lg, z, ACT.Abs).then_inc(s_lchain, 1)
                    act.wait_ge(s_lchain, chain["l"])
                    chain["l"] += 1
                    nc.scalar.activation(lg, lg, ACT.Exp, scale=-1.0).then_inc(s_lchain, 1)
                    act.wait_ge(s_lchain, chain["l"])
                    nc.scalar.activation(lg, lg, ACT.Ln, bias=ones[:, 0:1]).then_inc(s_log, 1)
                elif name == "att_exp":
                    m, = args
                    i = att_no[m]
                    act.wait_ge(s_sfx, i + 1)
                    if i > 1:
                        act.wait_ge(s_o, i - 1)
                    nc.scalar.activation(ab[:, i % 2, :], bank(("att", m))[:, :], ACT.Exp).then_inc(s_act_free, 1)
                elif name == "square_mix":
                    c, = args
                    act.wait_ge(s_o, att_no[(c, 1, 0)] + 1)
                    act.wait_ge(s_dve_free, freed_by[("proj", batch_of(c), len(proj_tiles()) - 1)][1])
                    if c > BATCHES[batch_of(c)][0]:
                        act.wait_ge(s_full, use_no[("turn_xn", c - 1, 1)] + 1)
                        act.wait_ge(s_spx, 32 * c)
                    nc.scalar.activation(xb[:, 1, 0:W], o_ps[:, :], ACT.Square)
                    nc.scalar.activation(xb[:, 1, W:2 * W].rearrange("p (j t) -> p j t", j=JW), ocT[:, :, span(c)],
                                         ACT.Square).then_inc(s_sq, 1)
                elif name == "root_mix":
                    c, = args
                    u = ("sum", c)
                    act.wait_ge(s_full, use_no[u] + 1)
                    if c > 0:
                        act.wait_ge(s_dve_free, freed_by[("out", c - 1, 1, 1)][1])
                    ss(nc.scalar.activation(st[:, 4:6], bank(u)[:, 0:2], ACT.Ln, bias=eps[:, 0:1], scale=1.0 / W))
                    nc.scalar.activation(st[:, 6:8], st[:, 4:6], ACT.Exp, scale=-0.5).then_inc(s_act_free, 1)
                elif name == "square_x2":
                    c, = args
                    act.wait_ge(s_dve_free, freed_by[("out", c, 1, 1)][1])
                    act.wait_ge(s_full, use_no[("sum", c)] + 1)
                    ss(nc.scalar.activation(xb[:, 1, :], xb[:, 0, :], ACT.Square, accum_out=st[:, 8:9]))
                    ss(nc.scalar.activation(st[:, 9:10], st[:, 8:9], ACT.Ln, bias=eps[:, 0:1], scale=1.0 / D))
                    nc.scalar.activation(st[:, 10:11], st[:, 9:10], ACT.Exp, scale=-0.5).then_inc(s_r2, 1)
                elif name == "store_xn":
                    c, = args
                    for i in range(2):
                        u = ("turn_xn", c, i)
                        act.wait_ge(s_full, use_no[u] + 1)
                        nc.scalar.activation(hT[:, 4 * i:4 * i + 4, span(c)],
                                             bank(u)[:, :].rearrange("p (k t) -> p k t", k=4), ACT.Copy)\
                            .then_inc(s_act_free, 1)
                elif name == "store_query":
                    bi, t = args
                    T = len(BATCHES[bi]) * P
                    u = ("query", bi, t)
                    act.wait_ge(s_full, use_no[u] + 1)
                    if t >= 2:
                        act.wait_ge(s_full, use_no[("key_scores", bi, t - 2)] + 1)
                    nc.scalar.activation(qt_tile(t)[:, 0:T], bank(u)[:, 0:T], ACT.Copy).then_inc(s_act_free, 1)
                elif name == "gate_exp":
                    c, h0 = args
                    n = heads_per_search(batch_of(c)) * TOPK
                    act.wait_ge(s_gd, search_no[(c, h0)])
                    nc.scalar.activation(gexp[:, 0:n], gdif[:, 0:n], ACT.Exp).then_inc(s_ge, 1)
                elif name == "final_root":
                    c, = args
                    act.wait_ge(s_fsum, c + 1)
                    ss(nc.scalar.activation(xn[:, c % 2, :], acc[:, c % 2, :], ACT.Square, accum_out=st[:, 11:12]))
                    ss(nc.scalar.activation(st[:, 12:13], st[:, 11:12], ACT.Ln, bias=eps[:, 0:1], scale=1.0 / D))
                    nc.scalar.activation(st[:, 13:14], st[:, 12:13], ACT.Exp, scale=-0.5).then_inc(s_fsq, 1)

            nc.scalar.preload_act_table_set("natural_log_exp_and_others")
            for i in range(4):
                act.wait_ge(s_full, i + 1)
                nc.scalar.activation(key_dst[:, 4 * i:4 * i + 4, :], bank(("turn_keys", i))[:, :], ACT.Copy)\
                    .then_inc(s_act_free, 1)
            for c, first, count in gather_line(group, front, "act"):
                with act.Fori(first, first + count) as i:
                    for q in range(2):
                        for part in range(PARTS):
                            group(c, i, q, part, False, False)

        @block.tensor
        def _(pe):
            def take(u):
                if before[u]:
                    freed(before[u])
                return bank(u)

            def w_tile(n):
                pe.wait_ge(s_w[n % WSLOTS], 16 * (n // WSLOTS + 1))
                return wpool[:, n % WSLOTS, :]

            def freed(u):
                eng, count = freed_by[u]
                pe.wait_ge(s_act_free if eng == "act" else s_dve_free, count)

            def group(c, i, q, part, first, last):
                if part != 2:
                    return
                n = i + c * BODIES
                if first and c > 0:
                    pe.wait_ge(s_fsum, c)
                wide = is_wide(c, i, q)
                first_wide = wide and 2 * i + q == wide_from[c]
                if first_wide:
                    pe.wait_ge(s_gain, BATCHES[batch_of(c) + 1][-1] + 1)
                pe.wait_ge(s_diag, n * 2 + q + 1)
                for s in range(GROUP):
                    ins = nc.tensor.matmul(vacc[:, :], diag[:, q, s, :], ring[:, q * GROUP + s, D:D + PE_COLS],
                                           start=first and s == 0, stop=last and s == GROUP - 1,
                                           skip_group_check=True)
                    if wide:
                        ins = nc.tensor.matmul(o_ps[:, :], diag[:, q, s, :], ring[:, q * GROUP + s, D + PE_COLS:2 * D],
                                               start=first_wide and s == 0, stop=last and s == GROUP - 1,
                                               skip_group_check=True)
                    ins.then_inc(s_vp, 1)

            def front(name, args):
                if name in ("turn_h", "turn_xn"):
                    c, = args
                    if name == "turn_h":
                        pe.wait_ge(s_hn, c + 1)
                    else:
                        pe.wait_ge(s_xn2, c + 1)
                    for i in range(2):
                        b = take((name, c, i))
                        for k in range(4):
                            ins = nc.tensor.transpose(b[:, k * P:(k + 1) * P],
                                                      xb[:, 1, (4 * i + k) * P:(4 * i + k + 1) * P], ident[:, :])
                        ins.then_inc(s_full, 1)
                elif name == "proj":
                    bi, t = args
                    kind, j = proj_tiles()[t]
                    chunks = BATCHES[bi]
                    T = len(chunks) * P
                    if t == 0:
                        freed(("turn_h", chunks[-1], 1))
                    b = take(("proj", bi, t))
                    w = w_tile(wt_proj(bi, t))
                    if kind == "v":
                        for lc in range(len(chunks)):
                            for k in range(KD):
                                ins = nc.tensor.matmul(b[:, lc * P:(lc + 1) * P], hT[:, k, lc * P:(lc + 1) * P],
                                                       w[:, k * P:(k + 1) * P], start=k == 0, stop=k == KD - 1)
                    else:
                        for k in range(KD):
                            ins = nc.tensor.matmul(b[:, 0:T], w[:, k * P:(k + 1) * P], hT[:, k, 0:T],
                                                   start=k == 0, stop=k == KD - 1)
                    ins.then_inc(s_full, 1)
                elif name == "att_z":
                    m, = args
                    c, half, kb = m
                    if half == 0 and kb == c:
                        freed(("proj", batch_of(c), proj_tiles().index(("v", JW - 1))))
                    b = take(("att", m))
                    rows = slice(half * DH, (half + 1) * DH)
                    for i in range(HEADS // 2):
                        ins = nc.tensor.matmul(b[:, i * P:(i + 1) * P], kT[rows, i, kb * P:(kb + 1) * P],
                                               qT[rows, i, span(c)], start=i == 0, stop=False,
                                               skip_group_check=True)
                    ins.then_inc(s_full, 1)
                elif name == "att_suffix":
                    m, = args
                    c, half, kb = m
                    n = att_no[m]
                    b = bank(("att", m))
                    pe.wait_ge(s_soft, n + 1)
                    if kb == c:
                        for i in range(4):
                            nc.tensor.matmul(b[:, i * P:(i + 1) * P], ident[:, :], bias_m[:, :], start=False,
                                             stop=False, skip_group_check=True)
                    else:
                        pe.wait_ge(s_carry, carry_no[(c, half, kb + 1)])
                        nc.tensor.matmul(b[:, :], neg_one[:, :].broadcast_to([P, P]), rs[:, 0:512], start=False, stop=False,
                                         skip_group_check=True)
                    nc.tensor.matmul(b[:, :], neg_tri[:, :], lb[:, n % 2, :], start=False, stop=True,
                                     skip_group_check=True).then_inc(s_sfx, 1)
                elif name == "att_out":
                    m, = args
                    c, half, kb = m
                    freed(("att", m))
                    if c > 0 and kb == c and half == 0:
                        pe.wait_ge(s_sq, c)
                        pe.wait_ge(s_gain, c)
                        if c == BATCHES[batch_of(c)][0]:
                            summed = [w for w in wide_from if w < BATCHES[batch_of(c) - 1][0]]
                            if summed:
                                pe.wait_ge(s_fsum, max(summed) + 1)
                    for i in range(4):
                        h = 2 * i + half
                        ins = nc.tensor.matmul(o_ps[half * DH:(half + 1) * DH, i * P:(i + 1) * P],
                                               vN[:, kb, h * DH:(h + 1) * DH],
                                               ab[:, att_no[m] % 2, i * P:(i + 1) * P],
                                               start=kb == c and i == 0, stop=kb == 0, skip_group_check=True)
                    ins.then_inc(s_o, 1)
                elif name == "sum_mix":
                    c, = args
                    pe.wait_ge(s_sq, c + 1)
                    b = take(("sum", c))
                    for part in range(2):
                        for j in range(JW):
                            o = (part * JW + j) * P
                            ins = nc.tensor.matmul(b[:, part:part + 1], xb[:, 1, o:o + P], ones[:, 0:1],
                                                   start=j == 0, stop=j == JW - 1)
                    ins.then_inc(s_full, 1)
                elif name == "out_proj":
                    c, n = args
                    pe.wait_ge(s_gain, c + 1)
                    for part in range(2):
                        b = take(("out", c, n, part))
                        src = (qT, ocT)[part]
                        for j in range(JW):
                            w = w_tile(wt_out(batch_of(c), part * JW + j))
                            ins = nc.tensor.matmul(b[:, :], src[:, j, span(c)], w[:, n * 512:(n + 1) * 512],
                                                   start=j == 0, stop=j == JW - 1)
                        ins.then_inc(s_full, 1)
                elif name == "query":
                    bi, t = args
                    T = len(BATCHES[bi]) * P
                    if t == 0:
                        freed(("turn_xn", BATCHES[bi][-1], 1))
                    b = take(("query", bi, t))
                    w = w_tile(wt_query(bi, t))
                    for k in range(KD):
                        ins = nc.tensor.matmul(b[:, 0:T], w[:, k * P:(k + 1) * P], hT[:, k, 0:T],
                                               start=k == 0, stop=k == KD - 1)
                    ins.then_inc(s_full, 1)
                elif name == "key_scores":
                    bi, t = args
                    if t == 0 and bi < KEYS_STAY:
                        freed(("turn_keys", 3))
                    elif t == 0:
                        pe.wait_ge(s_keysin, 16 * (bi - KEYS_STAY + 1))
                    keysT = key_dst if bi < KEYS_STAY else xbflat.rearrange("p (t n) -> p t n", t=LISTS)
                    freed(("query", bi, t))
                    b = take(("key_scores", bi, t))
                    for lc in range(len(BATCHES[bi])):
                        ins = nc.tensor.matmul(b[:, lc * P:(lc + 1) * P], qt_tile(t)[:, lc * P:(lc + 1) * P],
                                               keysT[:, t, :], start=True, stop=True)
                    ins.then_inc(s_full, 1)

            pe.wait_ge(s_pool, 8)
            pe.wait_ge(s_keyload, 32)
            for i in range(4):
                b = take(("turn_keys", i))
                for k in range(4):
                    ins = nc.tensor.transpose(b[:, k * P:(k + 1) * P], key_src[:, 4 * i + k, :], ident[:, :])
                ins.then_inc(s_full, 1)
            for c, first, count in gather_line(group, front, "pe"):
                with pe.Fori(first, first + count) as i:
                    for q in range(2):
                        for part in range(PARTS):
                            group(c, i, q, part, False, False)

        @block.vector
        def _(dve):
            n_tk = [0]
            n_mx = [0]

            def count(ins):
                n_tk[0] += 1
                ins.then_inc(s_tk, 1)

            def passed():
                dve.wait_ge(s_tk, n_tk[0])

            def tkc(ins):
                count(ins)
                passed()

            def group(c, i, q, part, first, last):
                n = i + c * BODIES
                G = n * 2 + q
                sl = slice(q * GROUP, (q + 1) * GROUP)
                if part == 2:
                    weights(G, sl)
                    if is_wide(c, i, q):
                        dve.sem_inc(s_vd, GROUP)
                    else:
                        add_rows(c, G, q, first)
                    return
                if first and part == 0:
                    dve.wait_ge(s_chunk[c % 2], 32 * (c // 2 + 1))
                half = q * GROUP + part * GROUP // 2
                for s in range(half, half + GROUP // 2):
                    dve.wait_ge(s_gat[s], (n + 1) * 16)
                    ins = nc.vector.tensor_tensor_reduce(out=ring[:, s, 0:D], in0=ring[:, s, 0:D],
                                                         in1=xn[:, c % 2, :], scale=1.0, scalar=0.0, op0=ALU.mult,
                                                         op1=ALU.add, accum_out=dots[:, s:s + 1])
                if part == 0:
                    return
                ins.then_inc(s_dot, 1)
                dve.wait_ge(s_dot, G + 1)
                xx = dots[:, sl]
                nc.vector.tensor_tensor(g_sq[:, sl], xx, xx, ALU.mult).then_inc(s_gsq, 1)
                nc.vector.tensor_tensor(g_xg[:, sl], xx, gate[:, c % KEEP, bass.ds(i * RING + q * GROUP, GROUP)],
                                        ALU.mult).then_inc(s_gxg, 1)
                dve.wait_ge(s_gsq, G + 1)
                nc.vector.scalar_tensor_tensor(out=g_cu[:, sl], in0=g_sq[:, sl], scalar=1.0 / GELU_CUBE, in1=xx,
                                               op0=ALU.add, op1=ALU.mult).then_inc(s_gcu, 1)

            def weights(G, sl):
                dve.wait_ge(s_gex, G + 1)
                nc.vector.tensor_scalar(g_de[:, sl], g_ex[:, sl], 1.0e30, 1.0, ALU.min, ALU.add).then_inc(s_gde, 1)
                dve.wait_ge(s_gde, G + 1)
                nc.vector.reciprocal(g_re[:, sl], g_de[:, sl]).then_inc(s_gre, 1)
                dve.wait_ge(s_gxg, G + 1)
                dve.wait_ge(s_gre, G + 1)
                nc.vector.tensor_tensor(g_w[:, sl], g_xg[:, sl], g_re[:, sl], ALU.mult).then_inc(s_gw, 1)

            def add_rows(c, G, q, first):
                dve.wait_ge(s_gw, G + 1)
                for k in range(GROUP):
                    if not (first and c == 0 and k == 0):
                        dve.wait_ge(s_vd, G * GROUP + k)
                    s = q * GROUP + k
                    nc.vector.scalar_tensor_tensor(out=acc[:, c % 2, PE_COLS:D], in0=ring[:, s, D + PE_COLS:2 * D],
                                                   scalar=g_w[:, s:s + 1], in1=acc[:, c % 2, PE_COLS:D],
                                                   op0=ALU.mult, op1=ALU.add).then_inc(s_vd, 1)

            def front(name, args):
                if name == "gate_h":
                    bi, j = args
                    T = len(BATCHES[bi]) * P
                    u = ("proj", bi, proj_tiles().index(("gc", j)))
                    hc = ("proj", bi, proj_tiles().index(("hc", j)))
                    dve.wait_ge(s_full, use_no[u] + 1)
                    dve.wait_ge(s_act_free, freed_by[hc][1])
                    if bi + j > 0:
                        dve.wait_ge(s_cv, 2 * (bi * JW + j))
                        before = (bi, j - 1) if j else (bi - 1, JW - 1)
                        gb = ("proj", before[0], proj_tiles().index(("gb", before[1])))
                        dve.wait_ge(s_dve_free, freed_by[gb][1])
                    if bi + j == 0:
                        dve.wait_ge(s_tail0, 1)
                    nc.vector.tensor_copy(cu[:, 0:2], tail[:, j, :])
                    nc.vector.tensor_tensor(cu[:, 2:2 + T], bank(u)[:, 0:T], hcs[:, 0:T], ALU.mult)\
                        .then_inc(s_dve_free, 1)
                    dve.wait_ge(s_dve_free, freed_by[u][1])
                    nc.vector.tensor_copy(tail[:, j, :], cu[:, T:T + 2]).then_inc(s_u, 1)
                elif name == "conv_taps":
                    bi, j = args
                    T = len(BATCHES[bi]) * P
                    u = ("proj", bi, proj_tiles().index(("gb", j)))
                    n = bi * JW + j
                    dve.wait_ge(s_tap2, n + 1)
                    nc.vector.scalar_tensor_tensor(out=ct[:, 0:T], in0=cu[:, 1:1 + T], scalar=cw[:, 1, j:j + 1],
                                                   in1=ct[:, 0:T], op0=ALU.mult, op1=ALU.add).then_inc(s_cv, 1)
                    dve.wait_ge(s_cv, 2 * n + 1)
                    nc.vector.scalar_tensor_tensor(out=ct[:, 0:T], in0=cu[:, 0:T], scalar=cw[:, 0, j:j + 1],
                                                   in1=ct[:, 0:T], op0=ALU.mult, op1=ALU.add).then_inc(s_cv, 1)
                    dve.wait_ge(s_cv, 2 * n + 2)
                    dve.wait_ge(s_full, use_no[u] + 1)
                    nc.vector.tensor_tensor(ocT[:, j, 0:T], bank(u)[:, 0:T], ct[:, 0:T], ALU.mult)\
                        .then_inc(s_dve_free, 1)
                elif name == "att_soft":
                    m, = args
                    c, half, kb = m
                    n = att_no[m]
                    dve.wait_ge(s_log, n + 1)
                    if n >= 2:
                        dve.wait_ge(s_sfx, n - 1)
                        if att_list[n - 2][2] > 0:
                            dve.wait_ge(s_carry, carry_no[att_list[n - 2]])
                    ins = nc.vector.scalar_tensor_tensor(out=lb[:, n % 2, :], in0=bank(("att", m))[:, :], scalar=0.0,
                                                         in1=lt[:, n % 2, :], op0=ALU.max, op1=ALU.add)
                    if kb == c:
                        ins.then_inc(s_schain, 1)
                        n_mx[0] += 1
                        dve.wait_ge(s_schain, n_mx[0])
                        lv = lb[:, n % 2, :].rearrange("p (h t) -> p h t", h=4)
                        kv = keep01[:, :].rearrange("p (o t) -> p o t", o=1).broadcast_to([P, 4, P])
                        ins = nc.vector.tensor_tensor(lv, lv, kv, ALU.mult)
                    ins.then_inc(s_soft, 1)
                elif name == "att_carry":
                    m, = args
                    c, half, kb = m
                    n = att_no[m]
                    dve.wait_ge(s_soft, n + 1)
                    dve.wait_ge(s_sfx, n + 1)
                    if kb == c:
                        ins = nc.vector.tensor_copy(rs[:, 0:512], lb[:, n % 2, :])
                    else:
                        dve.wait_ge(s_carry, carry_no[(c, half, kb + 1)])
                        ins = nc.vector.tensor_tensor(rs[:, 0:512], rs[:, 0:512], lb[:, n % 2, :], ALU.add)
                    ins.then_inc(s_carry, 1)
                elif name == "gain_mix":
                    c, = args
                    dve.wait_ge(s_sq, c + 1)
                    for part, (src, dst) in enumerate(((o_ps[:, :].rearrange("p (j t) -> p j t", j=JW),
                                                        qT[:, :, span(c)]),
                                                       (ocT[:, :, span(c)], ocT[:, :, span(c)]))):
                        gv = ga[:, part, :].rearrange("p (j o) -> p j o", o=1).broadcast_to([P, JW, P])
                        ins = nc.vector.tensor_tensor(dst, src, gv, ALU.mult)
                    ins.then_inc(s_gain, 1)
                elif name == "add_mix":
                    c, n = args
                    cols = slice(n * 512, (n + 1) * 512)
                    if n == 0:
                        dve.wait_ge(s_act_free, freed_by[("sum", c)][1])
                        if c > 0:
                            dve.wait_ge(s_x, 16 * x_loads[("load_x_again", c)])
                    for part in range(2):
                        u = ("out", c, n, part)
                        dve.wait_ge(s_full, use_no[u] + 1)
                        if part:
                            dve.wait_ge(s_dve_free, freed_by[("out", c, n, 0)][1])
                        ins = nc.vector.scalar_tensor_tensor(out=xb[:, 0, cols], in0=bank(u)[:, :],
                                                             scalar=st[:, 6 + part:7 + part], in1=xb[:, 0, cols],
                                                             op0=ALU.mult, op1=ALU.add)
                        ins.then_inc(s_dve_free, 1)
                elif name == "norm_x2":
                    c, = args
                    dve.wait_ge(s_r2, c + 1)
                    if c == 0:
                        dve.wait_ge(s_fgain, 16)
                    nc.vector.scalar_tensor_tensor(out=xb[:, 1, :], in0=xb[:, 0, :], scalar=st[:, 10:11],
                                                   in1=ffn_gain[:, :], op0=ALU.mult, op1=ALU.mult).then_inc(s_xn2, 1)
                elif name == "top_keys":
                    bi, t = args
                    u = ("key_scores", bi, t)
                    h, half = t // 2, t % 2
                    dve.wait_ge(s_full, use_no[u] + 1)
                    lists = []
                    for lc, c in enumerate(BATCHES[bi]):
                        v, ix = tk(c, half, 0, h), tk(c, half, 1, h).bitcast(U32)
                        lists.append((bank(u)[:, lc * P:(lc + 1) * P], lt[:, 0, lc * P:(lc + 1) * P], v, ix))
                    for sc, left, v, ix in lists:
                        ins = nc.vector.max(out=v[:, 0:8], in_=sc)
                    tkc(ins)
                    for sc, left, v, ix in lists:
                        ins = nc.vector.match_replace(out=left, in_to_replace=v[:, 0:8], in_values=sc,
                                                      imm_value=LOWEST)
                    count(ins)
                    for sc, left, v, ix in lists:
                        nc.vector.max_index(out=ix[:, 0:8], in_max=v[:, 0:8], in_values=sc)
                    passed()
                    for sc, left, v, ix in lists:
                        ins = nc.vector.max(out=v[:, 8:16], in_=left)
                    tkc(ins)
                    for sc, left, v, ix in lists:
                        ins = nc.vector.max_index(out=ix[:, 8:16], in_max=v[:, 8:16], in_values=left)
                    ins.then_inc(s_dve_free, 1)
                elif name == "pair_sums":
                    c, h0 = args
                    bi = batch_of(c)
                    hs = heads_per_search(bi)
                    dve.wait_ge(s_dve_free, freed_by[("key_scores", bi, 2 * (h0 + hs) - 1)][1])
                    if search_no[(c, h0)] > 1:
                        dve.wait_ge(s_exp, search_no[(c, h0)] - 1)
                    n = hs * TOPK
                    v1, v2 = (tk(c, i, 0)[:, h0 * TOPK:h0 * TOPK + n] for i in range(2))
                    v1 = v1.rearrange("p (h a o) -> p h a o", h=hs, o=1).broadcast_to([P, hs, TOPK, TOPK])
                    v2 = v2.rearrange("p (h o b) -> p h o b", h=hs, o=1).broadcast_to([P, hs, TOPK, TOPK])
                    cand = big(c)[0][:, 0:hs * NPAIR]
                    tkc(nc.vector.tensor_tensor(cand.rearrange("p (h a b) -> p h a b", h=hs, a=TOPK), v1, v2, ALU.add))
                elif name == "top_pairs":
                    c, h0, first = args
                    heads = []
                    for i in (first, first + 1):
                        o = i * TOPK
                        heads.append((big(c)[0][:, i * NPAIR:(i + 1) * NPAIR],
                                      left_pairs[:, i * NPAIR:(i + 1) * NPAIR], best[:, o:o + TOPK],
                                      pos[:, o:o + TOPK]))
                    for cv, left, v, ix in heads:
                        ins = nc.vector.max(out=v[:, 0:8], in_=cv)
                    tkc(ins)
                    for cv, left, v, ix in heads:
                        ins = nc.vector.match_replace(out=left, in_to_replace=v[:, 0:8], in_values=cv,
                                                      imm_value=LOWEST)
                    count(ins)
                    for cv, left, v, ix in heads:
                        nc.vector.max_index(out=ix[:, 0:8], in_max=v[:, 0:8], in_values=cv)
                    passed()
                    for cv, left, v, ix in heads:
                        ins = nc.vector.max(out=v[:, 8:16], in_=left)
                    tkc(ins)
                    for cv, left, v, ix in heads:
                        ins = nc.vector.max_index(out=ix[:, 8:16], in_max=v[:, 8:16], in_values=left)
                    tkc(ins)
                elif name == "gate_start":
                    c, h0 = args
                    hs = heads_per_search(batch_of(c))
                    n = hs * TOPK
                    bv = best[:, 0:n].rearrange("p (h k) -> p h k", h=hs)
                    nc.vector.tensor_tensor(gdif[:, 0:n].rearrange("p (h k) -> p h k", h=hs), bv,
                                            bv[:, :, 0:1].broadcast_to([P, hs, TOPK]), ALU.subtract).then_inc(s_gd, 1)
                    nc.vector.tensor_scalar(pos_ab[:, 0:n], pos[:, 0:n], 4, None, ALU.logical_shift_right)
                    count(nc.vector.tensor_scalar(pos_ab[:, n:2 * n], pos[:, 0:n], 15, None, ALU.bitwise_and))
                    for i in range(2):
                        ins = nc.vector.tensor_copy(idx_f[:, i * n:(i + 1) * n],
                                                    tk(c, i, 1)[:, h0 * TOPK:h0 * TOPK + n].bitcast(U32))
                    passed()
                    tkc(nc.vector.tensor_copy(pos_f[:, 0:2 * n], pos_ab[:, 0:2 * n]))
                elif name == "look_up":
                    c, h0 = args
                    hs = heads_per_search(batch_of(c))
                    n = 2 * hs * TOPK
                    onehot, picked = (r.bitcast(BF16)[:, 0:n * TOPK] for r in big(c))
                    pv = pos_f[:, 0:n].rearrange("p (s o) -> p s o", o=1).broadcast_to([P, n, TOPK])
                    iv = iota16[:, :].rearrange("p (o a) -> p o a", o=1).broadcast_to([P, n, TOPK])
                    tkc(nc.vector.tensor_tensor(onehot.rearrange("p (s a) -> p s a", a=TOPK), pv, iv, ALU.is_equal))
                    lv = idx_f[:, 0:n].rearrange("p (h o a) -> p h o a", h=2 * hs, o=1)\
                        .broadcast_to([P, 2 * hs, TOPK, TOPK])
                    tkc(nc.vector.tensor_tensor(picked.rearrange("p (h k a) -> p h k a", h=2 * hs, k=TOPK),
                                                onehot.rearrange("p (h k a) -> p h k a", h=2 * hs, k=TOPK), lv,
                                                ALU.mult))
                    tkc(nc.vector.tensor_reduce(num[:, 0:n], picked.rearrange("p (s a) -> p s a", a=TOPK), AX_X,
                                                ALU.add))
                elif name == "experts":
                    c, h0 = args
                    hs = heads_per_search(batch_of(c))
                    n = hs * TOPK
                    to = slice(h0 * TOPK, h0 * TOPK + n)
                    if c >= KEEP:
                        dve.wait_ge(s_idx, (c - KEEP + 1) * GROUPS)
                    dve.wait_ge(s_ge, search_no[(c, h0)])
                    ev = gexp[:, 0:n].rearrange("p (h k) -> p h k", h=hs)
                    count(nc.vector.tensor_reduce(gs[:, 1, 0:hs], ev, AX_X, ALU.add))
                    nc.vector.scalar_tensor_tensor(out=idx[:, c % KEEP, to], in0=num[:, 0:n], scalar=float(NKEYS),
                                                   in1=num[:, n:2 * n], op0=ALU.mult, op1=ALU.add)
                    passed()
                    tkc(nc.vector.reciprocal(gs[:, 2, 0:hs], gs[:, 1, 0:hs]))
                    nc.vector.tensor_tensor(gate[:, c % KEEP, to].rearrange("p (h k) -> p h k", h=hs), ev,
                                            gs[:, 2, 0:hs].rearrange("p (h o) -> p h o", o=1)
                                            .broadcast_to([P, hs, TOPK]), ALU.mult).then_inc(s_exp, 1)
                elif name == "final_sum":
                    c, = args
                    dve.wait_ge(s_vp, (c + 1) * SLOTS)
                    dve.wait_ge(s_vd, (c + 1) * SLOTS)
                    if c in wide_from:
                        nc.vector.tensor_tensor(acc[:, c % 2, PE_COLS:D], o_ps[:, :], acc[:, c % 2, PE_COLS:D],
                                                ALU.add)
                    nc.vector.tensor_tensor(acc[:, c % 2, 0:PE_COLS], vacc[:, :], acc[:, c % 2, 0:PE_COLS], ALU.add)\
                        .then_inc(s_fsum, 1)
                elif name == "final_scale":
                    c, = args
                    dve.wait_ge(s_fsq, c + 1)
                    dve.wait_ge(s_fg, 16 * (c + 1))
                    nc.vector.scalar_tensor_tensor(out=acc[:, c % 2, :], in0=acc[:, c % 2, :], scalar=st[:, 13:14],
                                                   in1=xn[:, c % 2, :], op0=ALU.mult, op1=ALU.mult).then_inc(s_y, 1)

            nc.vector.memset(tail[:, :, :], 0.0).then_inc(s_tail0, 1)
            for c, first, count in gather_line(group, front, "dve"):
                with dve.Fori(first, first + count) as i:
                    for q in range(2):
                        for part in range(PARTS):
                            group(c, i, q, part, False, False)


_ARGS = ["x", "w_in", "w_out", "peer_wq", "peer_keys", "uv", "cols", "ffn_norm_g", "final_norm_g"]


def kernel(**inputs):
    import numpy as _np
    import concourse.bacc as _bacc
    from concourse.bass_utils import run_bass_kernel_spmd as _run

    nc = _bacc.Bacc("TRN2", target_bir_lowering=False, num_devices=1)
    data = {k: _np.asarray(v) for k, v in inputs.items()}
    data["uv"] = _np.concatenate([data["peer_u"][0], data["peer_v"][0]], axis=1)
    rows = [data["mix_norm_g"], data["attn_out_g"], data["conv_out_g"], data["conv_w"][0], data["conv_b"]]
    data["cols"] = _np.concatenate([r.reshape(-1, P).T for r in rows], axis=1)
    data["final_norm_g"] = data["final_norm_g"].reshape(1, -1)
    arrays, args = {}, []
    for name in _ARGS:
        a = _np.ascontiguousarray(data[name])
        arrays[f"in_{name}"] = a
        args.append(nc.dram_tensor(f"in_{name}", a.shape, mybir.dt.from_np(a.dtype), kind="ExternalInput").ap())
    out = nc.dram_tensor("out", (1, S, D), F32, kind="ExternalOutput").ap()
    build(nc, *args, out)
    r = _run(nc, [arrays], core_ids=[0])
    return r.results[0]["out"]
```
